# Optimizing a Trainium2 kernel written in Bass

```python
import math
import jax, jax.numpy as jnp
from jax import lax
import numpy as np

D_MODEL = 2048
BATCH = 1
SEQ = 256
DEPTH = 2

D_MIX = D_MODEL
GLA_WIDTH = D_MIX // 2
DIFF_WIDTH = D_MIX - GLA_WIDTH
GLA_HEADS = 4
GLA_KEY_WIDTH = GLA_WIDTH // 2
GLA_HEAD_K = GLA_KEY_WIDTH // GLA_HEADS
GLA_HEAD_V = GLA_WIDTH // GLA_HEADS
GLA_GATE_RANK = 16
GLA_GATE_TAU = 16.0
GLA_CHUNK = 64
DIFF_HEAD_DIM = 128
DIFF_HEADS = DIFF_WIDTH // (2 * DIFF_HEAD_DIM)
Q_BLOCK = 128
ROPE_THETA = 10000.0
D_FF = 4 * D_MODEL
NORM_EPS = 1e-6
SUBLN_EPS = 1e-5

IN_SIZES = (GLA_KEY_WIDTH, GLA_KEY_WIDTH, GLA_WIDTH, GLA_WIDTH, GLA_GATE_RANK,
            DIFF_HEADS * 2 * DIFF_HEAD_DIM, DIFF_HEADS * 2 * DIFF_HEAD_DIM, DIFF_WIDTH)
IN_COLS = sum(IN_SIZES)

kernel_name = "hymba_style_gla_diffattn_hybrid"

def rms_norm(x, w, eps):
    xf = x.astype(jnp.float32)
    y = xf * lax.rsqrt(jnp.mean(xf * xf, axis=-1, keepdims=True) + eps)
    return (y * w.astype(jnp.float32)).astype(x.dtype)

def rope_tables(positions, dim):
    inv_freq = ROPE_THETA ** (-jnp.arange(0, dim, 2, dtype=jnp.float32) / dim)
    ang = positions.astype(jnp.float32)[..., None] * inv_freq
    return jnp.cos(ang), jnp.sin(ang)

def apply_rope(t, cos, sin):
    half = t.shape[-1] // 2
    t1, t2 = t[..., :half], t[..., half:]
    c, s = cos.astype(t.dtype), sin.astype(t.dtype)
    return jnp.concatenate([t1 * c - t2 * s, t1 * s + t2 * c], axis=-1)

def lambda_init_fn(layer_idx):
    return 0.8 - 0.6 * math.exp(-0.3 * layer_idx)

def gla_mixer(q, k, v, g, gate_lr, gate_w2, gate_b, out_norm_w):
    B, S, _ = q.shape
    H, dk, dv, C = GLA_HEADS, GLA_HEAD_K, GLA_HEAD_V, GLA_CHUNK
    N = S // C
    log_alpha = jax.nn.log_sigmoid((gate_lr @ gate_w2 + gate_b).astype(jnp.float32)) / GLA_GATE_TAU

    def chunks(t, d):
        return t.reshape(B, N, C, H, d).transpose(1, 0, 3, 2, 4)

    qc = chunks(q * (dk ** -0.5), dk)
    kc = chunks(k, dk)
    vc = chunks(v, dv)
    bc = jnp.cumsum(chunks(log_alpha, dk), axis=3)
    causal = jnp.tril(jnp.ones((C, C), dtype=bool))[:, :, None]

    def step(state, inp):
        q_i, k_i, v_i, b_i = inp
        o_inter = jnp.einsum('bhcd,bhdv->bhcv', q_i * jnp.exp(b_i), state)
        rel = b_i[:, :, :, None, :] - b_i[:, :, None, :, :]
        decay = jnp.exp(jnp.where(causal, rel, -jnp.inf))
        attn = jnp.einsum('bhid,bhjd,bhijd->bhij', q_i, k_i, decay)
        o_intra = jnp.einsum('bhij,bhjv->bhiv', attn, v_i)
        b_last = b_i[:, :, -1:, :]
        k_dec = k_i * jnp.exp(b_last - b_i)
        new_state = (state * jnp.exp(b_last)[:, :, 0, :, None]
                     + jnp.einsum('bhcd,bhcv->bhdv', k_dec, v_i)).astype(jnp.float32)
        return new_state, (o_inter + o_intra).astype(jnp.float32)

    state0 = jnp.zeros((B, H, dk, dv), dtype=jnp.float32)
    _, o = lax.scan(step, state0, (qc, kc, vc, bc))
    o = o.transpose(1, 0, 3, 2, 4).reshape(B, S, H, dv)
    o = rms_norm(o, out_norm_w, NORM_EPS) * jax.nn.silu(g.reshape(B, S, H, dv).astype(jnp.float32))
    return o.reshape(B, S, H * dv).astype(v.dtype)

def diff_attention(q, k, v, cos, sin, q_norm_w, k_norm_w, lam_q1, lam_k1, lam_q2, lam_k2,
                   subln_w, lam_init):
    B, S, _ = q.shape
    H, dh = DIFF_HEADS, DIFF_HEAD_DIM
    q = rms_norm(q.reshape(B, S, H, 2, dh), q_norm_w, NORM_EPS).transpose(0, 2, 3, 1, 4)
    k = rms_norm(k.reshape(B, S, H, 2, dh), k_norm_w, NORM_EPS).transpose(0, 2, 3, 1, 4)
    q = apply_rope(q, cos, sin)
    k = apply_rope(k, cos, sin)
    v = v.reshape(B, S, H, 2 * dh).transpose(0, 2, 1, 3)
    f32 = jnp.float32
    lam = (jnp.exp(jnp.sum(lam_q1.astype(f32) * lam_k1.astype(f32)))
           - jnp.exp(jnp.sum(lam_q2.astype(f32) * lam_k2.astype(f32))) + lam_init)
    scale = dh ** -0.5
    outs = []
    for blk in range(S // Q_BLOCK):
        start = blk * Q_BLOCK
        end = start + Q_BLOCK
        s = jnp.einsum('bhcqd,bhckd->bhcqk', q[:, :, :, start:end], k[:, :, :, :end]).astype(f32) * scale
        mask = (start + jnp.arange(Q_BLOCK))[:, None] >= jnp.arange(end)[None, :]
        p = jax.nn.softmax(jnp.where(mask, s, -jnp.inf), axis=-1)
        w = p[:, :, 0] - lam * p[:, :, 1]
        outs.append(jnp.einsum('bhqk,bhkd->bhqd', w.astype(v.dtype), v[:, :, :end]))
    o = jnp.concatenate(outs, axis=2)
    o = rms_norm(o, subln_w, SUBLN_EPS) * (1.0 - lam_init)
    return o.transpose(0, 2, 1, 3).reshape(B, S, H * 2 * dh)

def setup_inputs(seed: int = 0) -> dict:
    key = jax.random.key(seed)
    ks = jax.random.split(key, 20)

    def nrm(k, shape, scale):
        return jax.random.normal(k, shape, dtype=jnp.float32) * scale

    x = nrm(ks[0], (BATCH, SEQ, D_MODEL), 1.0)
    positions = (jnp.arange(SEQ, dtype=jnp.int32)[None, :]
                 + jax.random.randint(ks[1], (BATCH, 1), 0, 1024, dtype=jnp.int32))
    return {
        "x": x,
        "positions": positions,
        "attn_norm_w": 1.0 + nrm(ks[2], (DEPTH, D_MODEL), 0.02),
        "w_in": nrm(ks[3], (DEPTH, D_MODEL, IN_COLS), D_MODEL ** -0.5),
        "gla_gate_w2": nrm(ks[4], (DEPTH, GLA_GATE_RANK, GLA_KEY_WIDTH), GLA_GATE_RANK ** -0.5),
        "gla_gate_b": nrm(ks[5], (DEPTH, GLA_KEY_WIDTH), 0.1),
        "gla_out_norm_w": 1.0 + nrm(ks[6], (DEPTH, GLA_HEAD_V), 0.02),
        "diff_q_norm_w": 1.0 + nrm(ks[7], (DEPTH, DIFF_HEAD_DIM), 0.02),
        "diff_k_norm_w": 1.0 + nrm(ks[8], (DEPTH, DIFF_HEAD_DIM), 0.02),
        "diff_lambda_q1": nrm(ks[9], (DEPTH, DIFF_HEAD_DIM), 0.1),
        "diff_lambda_k1": nrm(ks[10], (DEPTH, DIFF_HEAD_DIM), 0.1),
        "diff_lambda_q2": nrm(ks[11], (DEPTH, DIFF_HEAD_DIM), 0.1),
        "diff_lambda_k2": nrm(ks[12], (DEPTH, DIFF_HEAD_DIM), 0.1),
        "diff_subln_w": 1.0 + nrm(ks[13], (DEPTH, 2 * DIFF_HEAD_DIM), 0.02),
        "w_out": nrm(ks[14], (DEPTH, D_MIX, D_MODEL), D_MIX ** -0.5),
        "mlp_norm_w": 1.0 + nrm(ks[15], (DEPTH, D_MODEL), 0.02),
        "w_up": nrm(ks[16], (DEPTH, D_MODEL, D_FF), D_MODEL ** -0.5),
        "w_down": nrm(ks[17], (DEPTH, D_FF, D_MODEL), D_FF ** -0.5),
    }

def reference(x, positions, attn_norm_w, w_in, gla_gate_w2, gla_gate_b, gla_out_norm_w,
              diff_q_norm_w, diff_k_norm_w, diff_lambda_q1, diff_lambda_k1, diff_lambda_q2,
              diff_lambda_k2, diff_subln_w, w_out, mlp_norm_w, w_up, w_down):
    cos, sin = rope_tables(positions, DIFF_HEAD_DIM)
    cos = cos[:, None, None]
    sin = sin[:, None, None]
    split_points = np.cumsum(IN_SIZES)[:-1].tolist()
    for layer in range(DEPTH):
        n = rms_norm(x, attn_norm_w[layer], NORM_EPS)
        proj = n @ w_in[layer]
        g_q, g_k, g_v, g_g, g_lr, d_q, d_k, d_v = jnp.split(proj, split_points, axis=-1)
        y_gla = gla_mixer(g_q, g_k, g_v, g_g, g_lr, gla_gate_w2[layer], gla_gate_b[layer],
                          gla_out_norm_w[layer])
        y_diff = diff_attention(d_q, d_k, d_v, cos, sin, diff_q_norm_w[layer], diff_k_norm_w[layer],
                                diff_lambda_q1[layer], diff_lambda_k1[layer],
                                diff_lambda_q2[layer], diff_lambda_k2[layer],
                                diff_subln_w[layer], lambda_init_fn(layer))
        mixed = jnp.concatenate([y_gla, y_diff], axis=-1)
        x = x + mixed @ w_out[layer]
        n = rms_norm(x, mlp_norm_w[layer], NORM_EPS)
        x = x + jnp.square(jax.nn.relu(n @ w_up[layer])) @ w_down[layer]
    return x


_drawn_inputs = setup_inputs


def setup_inputs(seed=0):
    import zlib

    import numpy as np

    out = dict(_drawn_inputs(seed))
    spreads = {}
    factors = {'gla_out_norm_w': 5.566,
     'diff_q_norm_w': 4.511,
     'diff_k_norm_w': 4.771,
     'diff_subln_w': 4.452}
    for name, (base, spread) in spreads.items():
        noise = np.random.default_rng([zlib.crc32(name.encode()), seed]).standard_normal(out[name].shape)
        drawn = base * np.exp(spread * noise) if base else spread * noise
        out[name] = __import__('jax').numpy.asarray(drawn.astype(out[name].dtype))
    for name, factor in factors.items():
        out[name] = (out[name] * factor).astype(out[name].dtype)
    return out
```

```python
import math

import numpy as np
import concourse.bass as bass
from concourse import mybir

F32 = mybir.dt.float32
F32R = mybir.dt.float32r
I32 = mybir.dt.int32
BF16 = mybir.dt.bfloat16
ALU = mybir.AluOpType
ACT = mybir.ActivationFunctionType
AXX = mybir.AxisListType.X

P = 128
D = 2048
SEQ = 256
DEPTH = 2
T = SEQ // P
KT = D // P
CW = 512
GH, DK, DV = 4, 128, 256
DH = 4
RANK = 16
D_FF = 4 * D
IN_COLS = 2 * GH * DK + 2 * GH * DV + RANK + 3 * 1024
LR_COL = 2 * GH * DK + 2 * GH * DV
TAU = 16.0
EPS, SUB_EPS = 1e-6, 1e-5
THETA = 10000.0
MASKED = -1e30
SCALE = 128 ** -0.5

SLOTS = 4
KP = 2
IN_CHUNK = KT // KP
HALF = IN_CHUNK // 2
IN_AT = [c * CW for c in range(LR_COL // CW)] + [LR_COL + RANK + c * CW for c in range(6)]
CHUNKS = [(IN_CHUNK * c, IN_CHUNK, 0) for c in range(12)]
CHUNKS += [(12 * IN_CHUNK + HALF * k, HALF, (k // 4) * (KT // 2)) for k in range(8)]
MIX_PIECES = 12 * IN_CHUNK + 8 * HALF
BLOCKS = 4
BLOCK_PIECES = 8 * IN_CHUNK
LAYER_PIECES = MIX_PIECES + BLOCKS * BLOCK_PIECES
BLOCK_CHUNKS = 8
LAYER_CHUNKS = len(CHUNKS) + BLOCKS * BLOCK_CHUNKS

USES = ["nw", "x0", "x1", "x2", "x3", "lr", "gq", "lr_back", "lrT", "z", "gk", "diag"]
USES += [f"level{n}" for n in range(8)]
USES += ["go0", "go1", "dq0", "gy0", "gy1", "dq1", "dk0", "score0", "dk1", "score1", "w0", "score2",
         "do0", "w1", "score3", "do1", "w2", "do2", "w3", "do3", "dy0", "dy1", "m0", "m1", "m2", "m3"]
HUSES = 4 * BLOCKS
NUSES = len(USES) + HUSES
PAIR = {u: n % 2 for n, u in enumerate(USES)}
NTH = {u: n // 2 + 1 for n, u in enumerate(USES)}
PER_PAIR = [(NUSES + 1 - p) // 2 for p in range(2)]
LEVEL_AT = [27, 30, 33, 37, 41, 45, 49, 52]
NORM_DMAS = 3
PARAM_DMAS = 11
STEPS = {"dve": 160, "act": 40, "pool": 64}


def build(nc, ins, out):
    (x_d, pos_d, anw_d, win_d, w2_d, gb_d, onw_d, qnw_d, knw_d, lq1_d, lk1_d, lq2_d, lk2_d, sub_d,
     wout_d, mnw_d, wup_d, wdn_d, ident_d, maskb_d, lmask_d, scanm_d, invf_d, lamc_d) = ins

    def sb(name, shape, dt=F32):
        return nc.alloc_sbuf_tensor(name, shape, dt)

    sem = nc.alloc_semaphore

    raw = sb("raw", [P, SLOTS, KP, CW])
    w_high = sb("w_high", [P, SLOTS, KP, CW], F32R)
    w_low = sb("w_low", [P, SLOTS, KP, CW], F32R)
    x = sb("x", [P, T, D])
    xt_high = sb("xt_high", [P, KT, SEQ], F32R)
    xt_low = sb("xt_low", [P, KT, SEQ], F32R)
    with nc.sbuf_tensor("gq_t", [P, GH, SEQ], F32) as gq_t, \
            nc.sbuf_tensor("gk_t", [P, GH, SEQ], F32) as gk_t, \
            nc.sbuf_tensor("decay", [P, GH, SEQ], F32) as decay, \
            nc.sbuf_tensor("expo", [P, 2, GH, SEQ], F32) as expo, \
            nc.sbuf_tensor("q_lev", [P, 2, GH * SEQ // 2], F32) as q_lev, \
            nc.sbuf_tensor("k_lev", [P, 2, GH, SEQ], F32) as k_lev:
        pass
    mt_high = sb("mt_high", [P, KT, SEQ], F32R)
    mt_low = sb("mt_low", [P, KT, SEQ], F32R)
    v = sb("v", [P, T, 1024])
    y = sb("y", [P, T, 1024])
    att = sb("att", [P, 1536])
    dq_t = sb("dq_t", [P, 2 * DH, SEQ])
    dk_t = sb("dk_t", [P, 2 * DH, SEQ])
    stage = sb("stage", [P, 2, T, CW])
    tmp = sb("tmp", [P, 2048])
    w_t = sb("w_t", [P, 2, 384])
    ident = sb("ident", [P, P])
    maskb = sb("maskb", [P, 384])
    lmask = sb("lmask", [P, 7 * 64 + P])
    scanm = sb("scanm", [P, SEQ])
    invf = sb("invf", [P, 64])
    pos = sb("pos", [P, T], I32)
    posf = sb("posf", [P, T])
    cosb = sb("cosb", [P, T, 64])
    sinb = sb("sinb", [P, T, 64])
    nsin = sb("nsin", [P, T, 64])
    rope_c = sb("rope_c", [P, 2, T, P])
    rope_s = sb("rope_s", [P, 2, T, P])
    neghalf = sb("neghalf", [P, 8])
    eps = sb("eps", [P, 8])
    sub_eps = sb("sub_eps", [P, 8])
    nw_rows = sb("nw_rows", [36, P])
    nwt = sb("nwt", [P, 36])
    w2 = sb("w2", [RANK, GH * DK])
    wlr = sb("wlr", [P, KT, RANK])
    onw = sb("onw", [P, DV])
    subw = sb("subw", [P, 256])
    qknw = sb("qknw", [P, 2, P])
    lamc = sb("lamc", [P, 2])
    lam_s = sb("lam_s", [P, 2])
    lam_e = sb("lam_e", [P, 2])
    nlam = sb("nlam", [P, 1])
    lr_s = sb("lr_s", [P, T, RANK])
    lr_t = sb("lr_t", [RANK, SEQ])
    xss = sb("xss", [P, T])
    xrs0 = sb("xrs0", [P, T])
    xrs = sb("xrs", [P, 2, T])
    gss = sb("gss", [P, T, GH])
    grs0 = sb("grs0", [P, T, GH])
    grs = sb("grs", [P, T, GH])
    dss = sb("dss", [P, 4, 8])
    drs0 = sb("drs0", [P, 4, 8])
    drs = sb("drs", [P, 4, 8])
    oss = sb("oss", [P, DH, T])
    ors0 = sb("ors0", [P, DH, T])
    ors = sb("ors", [P, DH, T])
    smax = sb("smax", [P, DH, 2, T])
    nmax = sb("nmax", [P, DH, 2, T])
    ssum = sb("ssum", [P, DH, 2, T])
    srec = sb("srec", [P, DH, 2, T])
    lrec = sb("lrec", [P, DH, T])
    junk = sb("junk", [P, 8, P], BF16)

    acc = [nc.alloc_psum_tensor(f"acc{n}", [P, T, CW], F32) for n in range(2)]
    side = [nc.alloc_psum_tensor(f"side{n}", [P, 1024], F32) for n in range(2)]

    raw_in = [sem(f"raw_in{s}") for s in range(SLOTS)]
    high_ready = sem("high_ready")
    low_ready = sem("low_ready")
    piece_used = sem("piece_used")
    acc_done = sem("acc_done")
    side_full = [sem(f"side_full{n}") for n in range(2)]
    side_done = [sem(f"side_done{n}") for n in range(2)]
    side_high = sem("side_high")
    const_in = sem("const_in")
    ident_in = sem("ident_in")
    x_in = [sem(f"x_in{c}") for c in range(4)]
    norms_in = sem("norms_in")
    params_in = sem("params_in")
    out_in = sem("out_in")
    angle_ready = sem("angle_ready")
    sin_ready = sem("sin_ready")
    trig_ready = sem("trig_ready")
    const_ready = sem("const_ready")
    lam_sum = sem("lam_sum")
    lam_exp = sem("lam_exp")
    wlr_h = sem("wlr_h")
    wlr_ready = sem("wlr_ready")
    x_ss = sem("x_ss")
    x_rs = sem("x_rs")
    att_zero = sem("att_zero")
    z_abs = sem("z_abs")
    lev_arg = sem("lev_arg")
    lev_exp = sem("lev_exp")
    lev_ready = sem("lev_ready")
    gate_exp = sem("gate_exp")
    gate_rec = sem("gate_rec")
    gate_ready = sem("gate_ready")
    g_ss = sem("g_ss")
    g_rs = sem("g_rs")
    qk_ss = sem("qk_ss")
    rope_ready = sem("rope_ready")
    smax_ready = sem("smax_ready")
    exp_ready = sem("exp_ready")
    w_ready = sem("w_ready")
    o_ss = sem("o_ss")
    o_rs = sem("o_rs")
    relu_h = sem("relu_h")
    merge_open = sem("merge_open")
    layer_open = sem("layer_open")
    load_open = sem("load_open")
    dve_step = sem("dve_step")
    act_step = sem("act_step")
    pool_step = sem("pool_step")

    def full(u, layer):
        return side_full[PAIR[u]], layer * PER_PAIR[PAIR[u]] + NTH[u]

    def done(u, layer):
        return side_done[PAIR[u]], layer * PER_PAIR[PAIR[u]] + (NTH[u] + 1)

    def hpair(c):
        return (len(USES) + c) % 2

    def hnth(c, block, layer):
        p = hpair(c)
        first = (len(USES) + 1 - p) // 2 + c // 2 + 1
        return layer * PER_PAIR[p] + block * 2 + first

    class Chain:

        def __init__(self, eng, step, per_layer):
            self.eng, self.step, self.per_layer = eng, step, per_layer
            self.layer, self.before, self.n = 0, 0, 0

        def start_layer(self, layer, before):
            self.layer, self.before, self.n = layer, before, 0

        def __call__(self, ins):
            self.n += 1
            assert self.n <= self.per_layer
            ins.then_inc(self.step, 1)
            self.eng.wait_ge(self.step, self.layer * self.per_layer + (self.before + self.n))

        def end_layer(self):
            if self.per_layer > self.n:
                self.eng.sem_inc(self.step, self.per_layer - self.n)

    def flat(t):
        return t.rearrange("p a b -> p (a b)")

    def halves(t, s):
        b = t.rearrange("p (n two s) -> p n two s", two=2, s=s)
        n = 1024 // (2 * s)
        return b[:, :, 0, :], b[:, :, 1, :], b[:, :, 0, s - 1:s].broadcast_to([P, n, s])

    with nc.Block() as block:

        @block.sync
        def _(sp):
            sp.dma_start(ident[:], ident_d).then_inc(ident_in, 16)
            win = win_d.rearrange("l (k p) n -> l p k n", p=P)
            wout = wout_d.rearrange("l (k p) n -> l p k n", p=P)
            wup = wup_d.rearrange("l (k p) n -> l p k n", p=P)
            wdn = wdn_d.rearrange("l (k p) n -> l p k n", p=P)

            def load(n, before, src):
                sp.wait_ge(low_ready, before + (n + 1))
                if n == 0:
                    sp.sem_inc(load_open, 1)
                sp.dma_start(raw[:, n % SLOTS], src).then_inc(raw_in[n % SLOTS], 16)

            with sp.Fori(0, DEPTH) as layer:
                sp.wait_ge(piece_used, layer * (LAYER_PIECES - 6 * SLOTS) + 1)

                def bc(ap):
                    return ap.partition_broadcast(P)
                for dst, src in (
                        (nw_rows[0:16, :], anw_d[layer].rearrange("(k p) -> k p", p=P)),
                        (nw_rows[16:32, :], mnw_d[layer].rearrange("(k p) -> k p", p=P)),
                        (nw_rows[32:36, :], gb_d[layer].rearrange("(k p) -> k p", p=P))):
                    sp.dma_start(dst, src).then_inc(norms_in, 16)
                before = layer * LAYER_PIECES
                for n in range(SLOTS):
                    load(n, before, win[layer, :, KP * n:KP * (n + 1), IN_AT[0]:IN_AT[0] + CW])
                for dst, src in (
                        (wlr[:], win[layer, :, :, LR_COL:LR_COL + RANK]),
                        (w2[:], w2_d[layer]),
                        (onw[:], bc(onw_d[layer])), (subw[:], bc(sub_d[layer])),
                        (qknw[:, 0, :], bc(qnw_d[layer])), (qknw[:, 1, :], bc(knw_d[layer])),
                        (lamc[:], bc(lamc_d[layer])),
                        (tmp[:, 0:128], bc(lq1_d[layer])), (tmp[:, 128:256], bc(lq2_d[layer])),
                        (tmp[:, 256:384], bc(lk1_d[layer])), (tmp[:, 384:512], bc(lk2_d[layer]))):
                    sp.dma_start(dst, src).then_inc(params_in, 16)
                for c, (first, count, k0) in enumerate(CHUNKS):
                    for i in range(count):
                        k = k0 + KP * i
                        if first + i < SLOTS:
                            continue
                        if c < 12:
                            src = win[layer, :, k:k + KP, IN_AT[c]:IN_AT[c] + CW]
                        else:
                            at = (c - 12) % 4 * CW
                            src = wout[layer, :, k:k + KP, at:at + CW]
                        load(first + i, before, src)
                with sp.Fori(0, BLOCKS) as blk:
                    before = layer * LAYER_PIECES + blk * BLOCK_PIECES + MIX_PIECES
                    for c in range(8):
                        for i in range(IN_CHUNK):
                            k = KP * i
                            if c < 4:
                                src = wup[layer, :, k:k + KP, bass.ds(blk * (4 * CW) + c * CW, CW)]
                            else:
                                src = wdn[layer, :, bass.ds(blk * KT + k, KP),
                                          (c - 4) * CW:(c - 3) * CW]
                            load(IN_CHUNK * c + i, before, src)
            for c in range(4):
                sp.wait_ge(acc_done, 2 + DEPTH * LAYER_CHUNKS - 3 + c)
                sp.dma_start(out[0].rearrange("(t p) n -> p t n", p=P)[:, :, c * CW:(c + 1) * CW],
                             x[:, :, c * CW:(c + 1) * CW]).then_inc(out_in, 16)
            sp.wait_ge(out_in, 64)

        @block.tensor
        def _(pe):
            pe.sem_inc(piece_used, SLOTS)

            def piece(n, before, first, count, k0, left, parity, cidx):
                high, low = left
                i = n - first
                if i == 0:
                    pe.wait_ge(acc_done, cidx)
                pe.wait_ge(low_ready, before + (n + 1 + SLOTS))
                s = n % SLOTS
                for kk in range(KP):
                    k = k0 + KP * i + kk
                    for t in range(T):
                        o = acc[parity][:, t, :]
                        a_high = high[:, k, t * P:(t + 1) * P]
                        a_low = low[:, k, t * P:(t + 1) * P]
                        start = i == 0 and kk == 0
                        stop = i == count - 1 and kk == KP - 1
                        pe.matmul(o, a_high, w_high[:, s, kk, :], start=start, stop=False)
                        pe.matmul(o, a_high, w_low[:, s, kk, :], start=False, stop=False)
                        last = pe.matmul(o, a_low, w_high[:, s, kk, :], start=False, stop=stop)
                last.then_inc(piece_used, 1)

            with pe.Fori(0, DEPTH) as layer:
                before = layer * LAYER_PIECES
                at = [0, 0]

                def pieces(upto, needs={}):
                    while at[0] < upto:
                        first, count, k0 = CHUNKS[at[1]]
                        if at[0] in needs:
                            pe.wait_ge(*done(needs[at[0]], layer))
                        left = (xt_high, xt_low) if at[1] < 12 else (mt_high, mt_low)
                        piece(at[0], before, first, count, k0, left, at[1] % 2,
                              layer * LAYER_CHUNKS + (at[1] + 1))
                        at[0] += 1
                        if at[0] == first + count:
                            at[1] += 1

                def open_side(u):
                    pe.wait_ge(side_done[PAIR[u]], layer * PER_PAIR[PAIR[u]] + NTH[u])
                    return side[PAIR[u]]

                def full_sem(u):
                    return side_full[PAIR[u]]

                def transpose_chunk(u, src):
                    s = open_side(u)
                    for j in range(4):
                        for t in range(T):
                            last = pe.transpose(s[:, j * SEQ + t * P:j * SEQ + (t + 1) * P],
                                                src[:, t, j * P:(j + 1) * P], ident[:])
                    last.then_inc(full_sem(u), 1)

                pe.wait_ge(norms_in, layer * (NORM_DMAS * 16) + NORM_DMAS * 16)
                s = open_side("nw")
                pe.sem_inc(layer_open, 1)
                pe.wait_ge(ident_in, 16)
                pe.transpose(s[:, 0:36], nw_rows[:], ident[0:36, 0:36]).then_inc(full_sem("nw"), 1)
                pe.wait_ge(acc_done, layer * LAYER_CHUNKS + 1)
                pe.wait_ge(x_in[0], 16)
                transpose_chunk("x0", x[:, :, 0:CW])
                pe.wait_ge(x_in[1], 16)
                transpose_chunk("x1", x[:, :, CW:2 * CW])
                pieces(2, {0: "x0"})
                pe.wait_ge(x_in[2], 16)
                transpose_chunk("x2", x[:, :, 2 * CW:3 * CW])
                pe.wait_ge(acc_done, layer * LAYER_CHUNKS + 2)
                pieces(4, {2: "x1"})
                pe.wait_ge(x_in[3], 16)
                transpose_chunk("x3", x[:, :, 3 * CW:4 * CW])
                pieces(8, {4: "x2", 6: "x3"})

                s = open_side("lr")
                pe.wait_ge(wlr_ready, layer + 1)
                for k in range(KT):
                    pe.matmul(s[:, 0:SEQ], mt_high[:, k, 0:P], xt_high[:, k, :], start=k == 0, stop=False)
                    pe.matmul(s[:, 0:SEQ], mt_high[:, k, 0:P], xt_low[:, k, :], start=False, stop=False)
                    last = pe.matmul(s[:, 0:SEQ], mt_low[:, k, 0:P], xt_high[:, k, :],
                                     start=False, stop=k == KT - 1)
                last.then_inc(full_sem("lr"), 1)
                pieces(10)

                def chunk_taken(c):
                    pe.wait_ge(acc_done, layer * LAYER_CHUNKS + (2 + c + 1))

                chunk_taken(0)
                transpose_chunk("gq", stage[:, 0])
                s = open_side("lr_back")
                pe.wait_ge(*done("lr", layer))
                for t in range(T):
                    last = pe.matmul(s[:, t * CW:t * CW + RANK], lr_t[:, t * P:(t + 1) * P],
                                     ident[0:RANK, 0:RANK], start=True, stop=True)
                last.then_inc(full_sem("lr_back"), 1)
                pieces(12)
                s = open_side("lrT")
                pe.wait_ge(*done("lr_back", layer))
                for t in range(T):
                    last = pe.transpose(s[0:RANK, t * P:(t + 1) * P], lr_s[:, t, :], ident[:])
                last.then_inc(full_sem("lrT"), 1)
                pieces(15)
                s = open_side("z")
                pe.wait_ge(params_in, layer * (PARAM_DMAS * 16) + PARAM_DMAS * 16)
                pe.wait_ge(*done("lrT", layer))
                for h in range(GH):
                    last = pe.matmul(s[:, h * SEQ:(h + 1) * SEQ], w2[:, h * DK:(h + 1) * DK], lr_t[:],
                                     start=True, stop=True)
                last.then_inc(full_sem("z"), 1)
                pieces(18)
                chunk_taken(1)
                transpose_chunk("gk", stage[:, 1])

                pieces(24)
                s = open_side("diag")
                pe.wait_ge(*done("gq", layer))
                pe.wait_ge(*done("gk", layer))
                for h in range(GH):
                    for t in range(T):
                        last = pe.matmul(s[:, (h * T + t) * P:(h * T + t + 1) * P],
                                         gk_t[:, h, t * P:(t + 1) * P], gq_t[:, h, t * P:(t + 1) * P],
                                         start=True, stop=True)
                last.then_inc(full_sem("diag"), 1)
                for n, a in enumerate(LEVEL_AT):
                    pieces(a + 3)
                    s = open_side(f"level{n}")
                    pe.wait_ge(lev_ready, layer * 8 + (n + 1))
                    for h in range(GH):
                        if n == 0:
                            last = pe.matmul(s[:, h * P:(h + 1) * P], k_lev[:, 0, h, 0:P],
                                             q_lev[:, 0, h * P:(h + 1) * P], start=True, stop=True)
                            continue
                        for t in range(T):
                            at64 = (h * T + t) * 64
                            last = pe.matmul(s[:, at64:at64 + 64],
                                             k_lev[:, n % 2, h, t * P:(t + 1) * P],
                                             q_lev[:, n % 2, at64:at64 + 64], start=True, stop=True)
                    last.then_inc(full_sem(f"level{n}"), 1)

                pieces(59)
                s = open_side("go0")
                pe.wait_ge(*done("level7", layer))
                pe.wait_ge(*done("level0", layer))
                chunk_taken(3)
                for h in range(GH):
                    last = pe.matmul(s[:, h * DV:(h + 1) * DV], att[:, 2 * h * P:(2 * h + 1) * P],
                                     v[:, 0, h * DV:(h + 1) * DV], start=True, stop=True)
                last.then_inc(full_sem("go0"), 1)
                s = open_side("go1")
                for h in range(GH):
                    o = s[:, h * DV:(h + 1) * DV]
                    pe.matmul(o, att[:, 1024 + h * P:1024 + (h + 1) * P], v[:, 0, h * DV:(h + 1) * DV],
                              start=True, stop=False)
                    last = pe.matmul(o, att[:, (2 * h + 1) * P:(2 * h + 2) * P],
                                     v[:, 1, h * DV:(h + 1) * DV], start=False, stop=True)
                last.then_inc(full_sem("go1"), 1)

                def turned(n):
                    pe.wait_ge(rope_ready, layer * 4 + (n + 1))

                pieces(66)
                turned(0)
                transpose_chunk("dq0", stage[:, 0])
                pieces(68)
                pe.wait_ge(*done("go0", layer))
                pe.wait_ge(*done("go1", layer))
                transpose_chunk("gy0", y[:, :, 0:CW])
                pieces(69)
                transpose_chunk("gy1", y[:, :, CW:2 * CW])
                pieces(72)
                turned(1)
                transpose_chunk("dq1", stage[:, 1])
                pieces(80)
                turned(2)
                transpose_chunk("dk0", stage[:, 0])

                def score(h):
                    s = open_side(f"score{h}")
                    for m in range(2):
                        o = s[:, m * CW:m * CW + 384]
                        q, k = dq_t[:, 2 * h + m, :], dk_t[:, 2 * h + m, :]
                        pe.matmul(o[:, 0:P], q[:, 0:P], k[:, 0:P], start=True, stop=True)
                        last = pe.matmul(o[:, P:384], q[:, P:SEQ], k, start=True, stop=True)
                    last.then_inc(full_sem(f"score{h}"), 1)

                def turn_weights(h):
                    s = open_side(f"w{h}")
                    pe.wait_ge(w_ready, layer * DH + (h + 1))
                    for j in range(3):
                        base = (h % 2) * 768
                        last = pe.transpose(s[:, j * P:(j + 1) * P],
                                            att[:, base + j * P:base + (j + 1) * P], ident[:])
                    last.then_inc(full_sem(f"w{h}"), 1)

                def head_out(h):
                    s = open_side(f"do{h}")
                    pe.wait_ge(*done(f"w{h}", layer))
                    chunk_taken(10 + h // 2)
                    w, cols = w_t[:, h % 2, :], slice(h * 256, (h + 1) * 256)
                    pe.matmul(s[:, 0:256], w[:, 0:P], v[:, 0, cols], start=True, stop=True)
                    pe.matmul(s[:, 256:512], w[:, P:2 * P], v[:, 0, cols], start=True, stop=False)
                    pe.matmul(s[:, 256:512], w[:, 2 * P:3 * P], v[:, 1, cols], start=False,
                              stop=True).then_inc(full_sem(f"do{h}"), 1)

                pieces(84)
                pe.wait_ge(*done("dq0", layer))
                pe.wait_ge(*done("dk0", layer))
                score(0)
                pieces(88)
                turned(3)
                transpose_chunk("dk1", stage[:, 1])
                score(1)
                pieces(89)
                turn_weights(0)
                pieces(92)
                pe.wait_ge(*done("dq1", layer))
                pe.wait_ge(*done("dk1", layer))
                score(2)
                pieces(93)
                head_out(0)
                pieces(94)
                turn_weights(1)
                pieces(96, {})
                score(3)
                pieces(97, {96: "gy0", 98: "gy1"})
                head_out(1)
                pieces(98)
                turn_weights(2)
                pieces(101, {98: "gy1"})
                head_out(2)
                pieces(102)
                turn_weights(3)
                pieces(105)
                head_out(3)
                pieces(106)
                pe.wait_ge(*done("do0", layer))
                pe.wait_ge(*done("do1", layer))
                transpose_chunk("dy0", y[:, :, 0:CW])
                pieces(110)
                pe.wait_ge(*done("do2", layer))
                pe.wait_ge(*done("do3", layer))
                transpose_chunk("dy1", y[:, :, CW:2 * CW])
                for c in range(3):
                    pieces(118 + 4 * c, {112: "dy0", 114: "dy1"})
                    chunk_taken(16 + c)
                    transpose_chunk(f"m{c}", x[:, :, c * CW:(c + 1) * CW])
                pieces(MIX_PIECES)

                def mlp_block(blk, is_first):
                    before = layer * LAYER_PIECES + blk * BLOCK_PIECES + MIX_PIECES
                    chunks = layer * LAYER_CHUNKS + blk * BLOCK_CHUNKS + len(CHUNKS)

                    def turn_inner(c):
                        p = hpair(c)
                        pe.wait_ge(side_done[p], hnth(c, blk, layer))
                        pe.wait_ge(relu_h, layer * HUSES + blk * 4 + (c + 1))
                        for j in range(4):
                            for t in range(T):
                                last = pe.transpose(
                                    side[p][:, j * SEQ + t * P:j * SEQ + (t + 1) * P],
                                    stage[:, c % 2, t, j * P:(j + 1) * P], ident[:])
                        last.then_inc(side_full[p], 1)

                    for c in range(8):
                        left = (xt_high, xt_low) if c < 4 else (mt_high, mt_low)
                        for i in range(IN_CHUNK):
                            if i == 2 and 1 <= c <= 4:
                                turn_inner(c - 1)
                            if i == 2 and c == 0 and is_first:
                                chunk_taken(19)
                                transpose_chunk("m3", x[:, :, 3 * CW:4 * CW])
                            if i % 2 == 0 and c == 0 and is_first:
                                pe.wait_ge(*done(f"m{i // 2}", layer))
                            if i % 2 == 0 and c == 4:
                                pe.wait_ge(side_done[hpair(i // 2)], hnth(i // 2, blk, layer) + 1)
                            piece(IN_CHUNK * c + i, before, IN_CHUNK * c, IN_CHUNK, 0, left, c % 2,
                                  chunks + (c + 1))

                mlp_block(0, True)
                with pe.Fori(1, BLOCKS) as blk:
                    mlp_block(blk, False)

        @block.scalar
        def _(act):
            for c in range(4):
                cols = slice(c * CW, (c + 1) * CW)
                act.dma_start(x[:, :, cols], x_d[0].rearrange("(t p) n -> p t n", p=P)[:, :, cols]
                              ).then_inc(x_in[c], 16)
            for dst, src in ((invf[:], invf_d), (lmask[:], lmask_d), (scanm[:], scanm_d),
                             (maskb[:], maskb_d)):
                act.dma_start(dst, src).then_inc(const_in, 16)
            act.dma_start(pos[:], pos_d[0].rearrange("(t p) -> p t", p=P),
                          allow_slow_non_contiguous=True).then_inc(const_in, 16)
            link = Chain(act, act_step, STEPS["act"])
            for p in range(2):
                act.sem_inc(side_done[p], 1)

            def split(n, before):
                act.wait_ge(raw_in[n % SLOTS], before * (16 // SLOTS) + (n // SLOTS + 1) * 16)
                act.wait_ge(piece_used, before + (n + 1))
                act.activation(w_high[:, n % SLOTS], raw[:, n % SLOTS], ACT.Copy).then_inc(high_ready, 1)

            with act.Fori(0, DEPTH) as layer:
                link.start_layer(layer, 0)
                at = [0]

                def pieces(upto):
                    while at[0] < upto:
                        split(at[0], layer * LAYER_PIECES)
                        at[0] += 1

                def source(u):
                    act.wait_ge(*full(u, layer))
                    return side[PAIR[u]]

                def done_sem(u):
                    return side_done[PAIR[u]]

                def squared(t):
                    return tmp[:].bitcast(BF16)[:, t * D:(t + 1) * D]

                def normed_high(u, c, w0):
                    s = source(u)
                    for j in range(4):
                        last = act.activation(xt_high[:, 4 * c + j, :], s[:, j * SEQ:(j + 1) * SEQ],
                                              ACT.Copy, scale=nwt[:, w0 + 4 * c + j:w0 + 4 * c + j + 1])
                    last.then_inc(side_high, 1)

                s = source("nw")
                act.activation(nwt[:], s[:, 0:36], ACT.Copy).then_inc(done_sem("nw"), 1)
                act.wait_ge(*done("nw", layer))
                normed_high("x0", 0, 0)
                pieces(2)
                normed_high("x1", 1, 0)
                pieces(4)
                normed_high("x2", 2, 0)
                act.wait_ge(const_ready, 1)
                act.wait_ge(params_in, layer * (PARAM_DMAS * 16) + PARAM_DMAS * 16)
                act.activation(mt_high[:, :, 0:RANK], wlr[:], ACT.Copy).then_inc(wlr_h, 1)
                pieces(6)
                normed_high("x3", 3, 0)
                pieces(8)
                act.wait_ge(lam_sum, layer + 1)
                act.activation(lam_e[:], lam_s[:], ACT.Exp).then_inc(lam_exp, 1)
                for c in range(4):
                    act.wait_ge(x_in[c], 16)
                act.wait_ge(acc_done, layer * LAYER_CHUNKS + 2)
                for t in range(T):
                    act.activation(squared(t), x[:, t, :], ACT.Square, scale=D ** -0.5,
                                   accum_out=xss[:, t:t + 1]).then_inc(x_ss, 1)
                    pieces(9 + t)

                pieces(12)
                s = source("lr")
                act.activation(lr_t[:], s[0:RANK, 0:SEQ], ACT.Copy).then_inc(done_sem("lr"), 1)
                pieces(14)
                s = source("gq")
                act.activation(flat(gq_t[:]), s[:], ACT.Copy).then_inc(done_sem("gq"), 1)
                pieces(16)
                s = source("lrT")
                act.activation(lr_t[:], s[0:RANK, 0:SEQ], ACT.Copy).then_inc(done_sem("lrT"), 1)
                pieces(19)
                act.wait_ge(*done("z", layer))
                e1 = flat(expo[:, 1])
                link(act.activation(e1, flat(decay[:]), ACT.Abs))
                pieces(20)
                link(act.activation(e1, e1, ACT.Exp, scale=-1.0))
                pieces(21)
                act.activation(e1, e1, ACT.Ln, bias=1.0).then_inc(z_abs, 1)
                pieces(22)
                s = source("gk")
                act.activation(flat(gk_t[:]), s[:], ACT.Copy).then_inc(done_sem("gk"), 1)

                pieces(24)
                act.wait_ge(angle_ready, layer + 1)
                act.activation(sinb[:], att[:, 1024:1152].rearrange("p (t f) -> p t f", t=T), ACT.Sin)
                act.activation(cosb[:], att[:, 1024:1152].rearrange("p (t f) -> p t f", t=T), ACT.Sin,
                               scale=0.5).then_inc(sin_ready, 1)

                def level_exp(n):
                    act.wait_ge(lev_arg, layer * 8 + (n + 1))
                    e = flat(expo[:, n % 2])
                    act.activation(e, e, ACT.Exp, scale=1.0 / TAU).then_inc(lev_exp, 1)

                def gate(c):
                    act.wait_ge(acc_done, layer * LAYER_CHUNKS + (2 + 4 + c + 1))
                    act.activation(stage[:, c], y[:, :, c * CW:(c + 1) * CW], ACT.Exp,
                                   scale=-1.0).then_inc(gate_exp, 1)

                for n, a in enumerate(LEVEL_AT):
                    pieces(a + 1)
                    level_exp(n)
                    if n == 1:
                        pieces(34)
                        s = source("level0")
                        act.activation(att[:, 1024:1536], s[:, 0:CW],
                                       ACT.Copy).then_inc(done_sem("level0"), 1)
                    if n == 5:
                        pieces(46)
                        gate(0)
                pieces(54)
                gate(1)

                def junk256(n):
                    return junk[:, 2 * n:2 * n + 2, :].rearrange("p a b -> p (a b)")

                def qk_squares(n):
                    if n == 0:
                        act.wait_ge(g_ss, layer * T + T)
                    else:
                        act.wait_ge(qk_ss, layer * 4 + n)
                    act.wait_ge(acc_done, layer * LAYER_CHUNKS + (2 + 6 + n + 1))
                    for t in range(T):
                        for j in range(4):
                            last = act.activation(junk[:, t * 4 + j, :], stage[:, n % 2, t, j * P:(j + 1) * P],
                                                  ACT.Square, scale=P ** -0.5,
                                                  accum_out=dss[:, n, t * 4 + j:t * 4 + j + 1])
                    last.then_inc(qk_ss, 1)

                def operand(u, k0):
                    s = source(u)
                    act.activation(mt_high[:, k0:k0 + 4, :].rearrange("p a b -> p (a b)"), s[:],
                                   ACT.Copy).then_inc(side_high, 1)

                def copy_qk(u, dst, c):
                    s = source(u)
                    act.activation(dst[:, 4 * c:4 * c + 4, :].rearrange("p a b -> p (a b)"), s[:],
                                   ACT.Copy).then_inc(done_sem(u), 1)

                for t in range(T):
                    pieces(62 + t)
                    s = source(f"go{t}")
                    if t:
                        act.wait_ge(g_ss, layer * T + t)
                    for h in range(GH):
                        last = act.activation(junk256(h), s[:, h * DV:(h + 1) * DV], ACT.Square,
                                              scale=DV ** -0.5, accum_out=gss[:, t, h:h + 1])
                    last.then_inc(g_ss, 1)
                qk_squares(0)
                pieces(69)
                qk_squares(1)
                pieces(70)
                copy_qk("dq0", dq_t, 0)
                pieces(72)
                operand("gy0", 0)
                pieces(73)
                operand("gy1", 4)
                pieces(76)
                copy_qk("dq1", dq_t, 1)
                pieces(77)
                qk_squares(2)
                pieces(83)
                copy_qk("dk0", dk_t, 0)
                pieces(85)
                qk_squares(3)

                def softmax_exp(h):
                    act.wait_ge(smax_ready, layer * DH + (h + 1))
                    base = (h % 2) * 768
                    for m in range(2):
                        for t in range(T):
                            a, b = base + m * 384 + (P if t else 0), base + m * 384 + (384 if t else P)
                            last = act.activation(att[:, a:b], att[:, a:b], ACT.Exp, scale=SCALE,
                                                  bias=nmax[:, h, m, t:t + 1],
                                                  accum_out=ssum[:, h, m, t:t + 1])
                    last.then_inc(exp_ready, 1)

                def copy_weights(h):
                    s = source(f"w{h}")
                    act.activation(w_t[:, h % 2, :], s[:, 0:384], ACT.Copy).then_inc(done_sem(f"w{h}"), 1)

                def out_squares(h):
                    s = source(f"do{h}")
                    if h:
                        act.wait_ge(o_ss, layer * DH + h)
                    for t in range(T):
                        last = act.activation(junk256(t), s[:, t * 256:(t + 1) * 256], ACT.Square,
                                              scale=256 ** -0.5, accum_out=oss[:, h, t:t + 1])
                    last.then_inc(o_ss, 1)

                pieces(88)
                softmax_exp(0)
                pieces(92)
                copy_qk("dk1", dk_t, 1)
                softmax_exp(1)
                pieces(93)
                copy_weights(0)
                pieces(96)
                softmax_exp(2)
                pieces(97)
                out_squares(0)
                pieces(98)
                copy_weights(1)
                pieces(101)
                softmax_exp(3)
                out_squares(1)
                pieces(102)
                copy_weights(2)
                pieces(105)
                out_squares(2)
                pieces(106)
                copy_weights(3)
                pieces(109)
                out_squares(3)
                pieces(110)
                operand("dy0", 8)
                pieces(113)
                operand("dy1", 12)
                pieces(122)
                normed_high("m0", 0, 16)
                pieces(126)
                normed_high("m1", 1, 16)
                pieces(MIX_PIECES)

                def mlp_block(blk, is_first):
                    before = layer * LAYER_PIECES + blk * BLOCK_PIECES + MIX_PIECES
                    chunks = layer * LAYER_CHUNKS + blk * BLOCK_CHUNKS + (len(CHUNKS) + 2)
                    for r in range(BLOCK_PIECES):
                        if is_first and r == 2:
                            normed_high("m2", 2, 16)
                        if is_first and r == 6:
                            normed_high("m3", 3, 16)
                        if is_first and r in (7, 8):
                            t = r - 7
                            act.wait_ge(acc_done, layer * LAYER_CHUNKS + (2 + len(CHUNKS)))
                            act.activation(squared(t), x[:, t, :], ACT.Square, scale=D ** -0.5,
                                           accum_out=xss[:, t:t + 1]).then_inc(x_ss, 1)
                        if r % 8 == 4 and 8 < r <= 36:
                            c = r // 8 - 1
                            act.wait_ge(acc_done, chunks + (c + 1))
                            act.activation(stage[:, c % 2], stage[:, c % 2],
                                           ACT.Square).then_inc(relu_h, 1)
                        if r % 8 == 6 and 8 < r <= 38:
                            c = r // 8 - 1
                            act.wait_ge(side_full[hpair(c)], hnth(c, blk, layer))
                            act.activation(mt_high[:, 4 * c:4 * c + 4, :].rearrange("p a b -> p (a b)"),
                                           side[hpair(c)][:], ACT.Copy).then_inc(side_high, 1)
                        split(r, before)

                mlp_block(0, True)
                with act.Fori(1, BLOCKS) as blk:
                    mlp_block(blk, False)
                link.end_layer()

        @block.vector
        def _(dve):
            link = Chain(dve, dve_step, STEPS["dve"])
            dve.sem_inc(low_ready, SLOTS)
            dve.sem_inc(acc_done, 2)

            def split(n, before):
                dve.wait_ge(high_ready, before + (n + 1))
                dve.tensor_tensor(w_low[:, n % SLOTS], raw[:, n % SLOTS],
                                  w_high[:, n % SLOTS].bitcast(F32), ALU.subtract).then_inc(low_ready, 1)

            with dve.Fori(0, DEPTH) as layer:
                link.start_layer(layer, 0)
                at = [0]

                def pieces(upto):
                    while at[0] < upto:
                        split(at[0], layer * LAYER_PIECES)
                        at[0] += 1

                def source(u):
                    dve.wait_ge(*full(u, layer))
                    return side[PAIR[u]]

                def done_sem(u):
                    return side_done[PAIR[u]]

                def normed_low(u, c, w0, nth):
                    s = source(u)
                    dve.wait_ge(side_high, layer * (len(OPERANDS) + HUSES) + nth)
                    for j in range(4):
                        k = 4 * c + j
                        last = dve.scalar_tensor_tensor(
                            out=xt_low[:, k, :], in0=s[:, j * SEQ:(j + 1) * SEQ],
                            scalar=nwt[:, w0 + k:w0 + k + 1], in1=xt_high[:, k, :].bitcast(F32),
                            op0=ALU.mult, op1=ALU.subtract)
                    last.then_inc(done_sem(u), 1)

                def operand(u, k0, nth):
                    s = source(u)
                    dve.wait_ge(side_high, layer * (len(OPERANDS) + HUSES) + nth)
                    dve.tensor_tensor(
                        mt_low[:, k0:k0 + 4, :].rearrange("p a b -> p (a b)"), s[:],
                        mt_high[:, k0:k0 + 4, :].rearrange("p a b -> p (a b)").bitcast(F32),
                        ALU.subtract).then_inc(done_sem(u), 1)

                def chunk_ready(c):
                    first, count, _ = CHUNKS[c]
                    dve.wait_ge(piece_used, layer * LAYER_PIECES + (SLOTS + first + count))

                def take(c, dst, times=None):
                    chunk_ready(c)
                    for t in range(T):
                        last = dve.tensor_scalar(dst[:, t, :], acc[c % 2][:, t, :], xrs[:, 0, t:t + 1],
                                                 times, ALU.mult, ALU.mult if times else ALU.bypass)
                    last.then_inc(acc_done, 1)

                def add_to_x(parity, c):
                    cols = x[:, :, c * CW:(c + 1) * CW]
                    dve.tensor_tensor(cols, acc[parity][:], cols, ALU.add).then_inc(acc_done, 1)

                normed_low("x0", 0, 0, 1)
                pieces(2)
                normed_low("x1", 1, 0, 2)
                dve.wait_ge(params_in, layer * (PARAM_DMAS * 16) + PARAM_DMAS * 16)
                link(dve.tensor_tensor(tmp[:, 512:768], tmp[:, 0:256], tmp[:, 256:512], ALU.mult))
                dve.reduce_sum(lam_s[:], tmp[:, 512:768].rearrange("p (a b) -> p a b", a=2),
                               axis=AXX).then_inc(lam_sum, 1)
                pieces(4)
                normed_low("x2", 2, 0, 3)
                dve.wait_ge(wlr_h, layer + 1)
                dve.tensor_tensor(mt_low[:, :, 0:RANK], wlr[:], mt_high[:, :, 0:RANK].bitcast(F32),
                                  ALU.subtract).then_inc(wlr_ready, 1)
                pieces(6)
                normed_low("x3", 3, 0, 4)
                pieces(10)
                dve.wait_ge(lam_exp, layer + 1)
                dve.scalar_tensor_tensor(out=nlam[:], in0=lam_e[:, 1:2], scalar=lamc[:, 0:1],
                                         in1=lam_e[:, 0:1], op0=ALU.subtract, op1=ALU.subtract)
                link(dve.tensor_scalar(subw[:], subw[:], lamc[:, 1:2], None, ALU.mult))

                pieces(12)
                dve.wait_ge(x_rs, layer * 2 + 1)
                take(0, stage[:, 0], DK ** -0.5)
                pieces(13)
                dve.wait_ge(const_in, 5 * 16)
                link(dve.tensor_copy(posf[:], pos[:]))
                ang = att[:, 1024:1152].rearrange("p (t f) -> p t f", t=T)
                turns = att[:, 1152:1280].rearrange("p (t f) -> p t f", t=T)
                whole = att[:, 1280:1408].bitcast(I32).rearrange("p (t f) -> p t f", t=T)
                for t in range(T):
                    last = dve.tensor_scalar(ang[:, t], invf[:], posf[:, t:t + 1], None, ALU.mult)
                link(last)
                link(dve.tensor_scalar(whole, ang, 1.0 / (2 * math.pi), None, ALU.mult))
                link(dve.tensor_copy(turns, whole))
                two_pi = 2 * math.pi
                c1 = 6.28125
                c2 = float(np.float32(np.round((two_pi - c1) * 2 ** 21) / 2 ** 21))
                c3 = float(np.float32(two_pi - c1 - c2))
                for c in (c1, c2, c3):
                    link(dve.scalar_tensor_tensor(out=ang, in0=turns, scalar=-c, in1=ang,
                                                  op0=ALU.mult, op1=ALU.add))
                pieces(14)
                s = source("lr_back")
                for t in range(T):
                    last = dve.tensor_scalar(lr_s[:, t, :], s[:, t * CW:t * CW + RANK],
                                             xrs[:, 0, t:t + 1], None, ALU.mult)
                last.then_inc(done_sem("lr_back"), 1)
                pieces(16)
                for op, by in ((ALU.is_gt, -two_pi), (ALU.is_lt, two_pi)):
                    edge = math.pi if by < 0 else -math.pi
                    link(dve.tensor_scalar(turns, ang, edge, by, op, ALU.mult))
                    link(dve.tensor_tensor(ang, ang, turns, ALU.add))
                dve.tensor_scalar(ang, ang, 3.1415925, -3.1415925, ALU.min, ALU.max).then_inc(angle_ready, 1)
                pieces(19)
                s = source("z")
                for h in range(GH):
                    last = dve.tensor_scalar(decay[:, h, :], s[:, h * SEQ:(h + 1) * SEQ],
                                             nwt[:, 32 + h:33 + h], None, ALU.add)
                last.then_inc(done_sem("z"), 1)
                pieces(20)
                take(1, stage[:, 1])
                pieces(23)
                dve.wait_ge(z_abs, layer + 1)
                link(dve.scalar_tensor_tensor(out=flat(expo[:, 0]), in0=flat(decay[:]), scalar=0.0,
                                              in1=flat(expo[:, 1]), op0=ALU.min, op1=ALU.subtract))
                pieces(25)
                for h in range(GH):
                    last = dve.tensor_tensor_scan(decay[:, h, :], scanm[:], expo[:, 0, h, :], 0.0,
                                                  ALU.mult, ALU.add)
                link(last)

                b4 = decay[:].rearrange("p h (c j) -> p h c j", j=64)

                def level_args(n):
                    if n >= 2:
                        dve.wait_ge(lev_ready, layer * 8 + (n - 1))
                    e = expo[:, n % 2]
                    if n == 0:
                        e4 = e.rearrange("p h (c j) -> p h c j", j=64)

                        def end(c):
                            return b4[:, :, c, 63:64].broadcast_to([P, GH, 64])
                        dve.tensor_copy(e4[:, :, 2, :], b4[:, :, 2, :])
                        dve.tensor_tensor(e4[:, :, 3, :], b4[:, :, 3, :], end(2), ALU.add)
                        dve.tensor_tensor(e4[:, :, 1, :], end(1), b4[:, :, 1, :], ALU.subtract)
                        link(dve.tensor_tensor(e4[:, :, 0, :], end(0), b4[:, :, 0, :], ALU.subtract))
                        dve.tensor_tensor(e4[:, :, 0, :], e4[:, :, 0, :], end(1),
                                          ALU.add).then_inc(lev_arg, 1)
                        return
                    half = P >> n
                    b_left, b_right, ref = halves(flat(decay[:]), half)
                    e_left, e_right, _ = halves(flat(e), half)
                    if n == 1:
                        dve.tensor_copy(e_right, b_right)
                    else:
                        dve.tensor_tensor(e_right, b_right, ref, ALU.subtract)
                    dve.tensor_tensor(e_left, ref, b_left, ALU.subtract).then_inc(lev_arg, 1)

                def merge(n):
                    s = source(f"level{n}")
                    half = P >> n
                    shape = [P, GH * T, 64 // half, half]
                    dst = att[:, 0:1024].rearrange("p (b m two s) -> p b m two s", b=GH * T, two=2,
                                                   s=half)[:, :, :, 1, :]
                    mask = lmask[:, (n - 1) * 64:n * 64].bitcast(I32).rearrange(
                        "p (o m s) -> p o m s", o=1, s=half).broadcast_to(shape)
                    data = s[:, 0:512].rearrange("p (b m s) -> p b m s", b=GH * T, s=half)
                    dve.sem_inc(merge_open, 1)
                    dve.copy_predicated(dst, mask, data).then_inc(done_sem(f"level{n}"), 1)

                def diagonal():
                    s = source("diag")
                    dve.wait_ge(att_zero, layer + 1)
                    mask = lmask[:, 448:576].bitcast(I32).rearrange("p (o i) -> p o i", o=1).broadcast_to(
                        [P, GH * T, P])
                    dve.sem_inc(merge_open, 1)
                    dve.copy_predicated(att[:, 0:1024].rearrange("p (b i) -> p b i", b=GH * T), mask,
                                        s[:].rearrange("p (b i) -> p b i", b=GH * T)
                                        ).then_inc(done_sem("diag"), 1)

                def gate_part(c, t):
                    if t == 0:
                        dve.wait_ge(gate_exp, layer * 2 + (c + 1))
                    part = stage[:, c, t, :]
                    link(dve.tensor_scalar(part, part, 1.0, None, ALU.add))
                    dve.reciprocal(part, part).then_inc(gate_rec, 1)

                pieces(27)
                level_args(0)
                pieces(28)
                take(2, v[:, :, 0:CW])
                diagonal()
                pieces(30)
                level_args(1)
                pieces(31)
                dve.wait_ge(sin_ready, layer + 1)
                link(dve.tensor_tensor(cosb[:], cosb[:], cosb[:], ALU.mult))
                dve.tensor_scalar(cosb[:], cosb[:], -2.0, 1.0, ALU.mult, ALU.add).then_inc(trig_ready, 1)
                dve.tensor_scalar(nsin[:], sinb[:], -1.0, None, ALU.mult).then_inc(trig_ready, 1)
                pieces(33)
                level_args(2)
                pieces(36)
                take(3, v[:, :, CW:1024])
                pieces(37)
                merge(1)
                level_args(3)
                pieces(40)
                merge(2)
                pieces(41)
                level_args(4)
                pieces(44)
                take(4, y[:, :, 0:CW])
                merge(3)
                pieces(45)
                level_args(5)
                pieces(47)
                gate_part(0, 0)
                pieces(48)
                merge(4)
                pieces(49)
                level_args(6)
                pieces(50)
                gate_part(0, 1)
                pieces(52)
                merge(5)
                take(5, y[:, :, CW:1024])
                pieces(53)
                level_args(7)
                pieces(55)
                gate_part(1, 0)
                pieces(56)
                merge(6)
                pieces(58)
                gate_part(1, 1)
                pieces(59)
                merge(7)
                pieces(60)
                dve.wait_ge(gate_ready, layer * 2 + 1)
                take(6, stage[:, 0])
                for t in range(T):
                    pieces(65 + t)
                    s = source(f"go{t}")
                    dve.wait_ge(g_rs, layer * T + (t + 1))
                    dve.wait_ge(gate_ready, layer * 2 + 2)
                    for h in range(GH):
                        cols = y[:, t, h * DV:(h + 1) * DV]
                        last = dve.scalar_tensor_tensor(out=cols, in0=s[:, h * DV:(h + 1) * DV],
                                                        scalar=grs[:, t, h:h + 1], in1=cols,
                                                        op0=ALU.mult, op1=ALU.mult)
                    last.then_inc(done_sem(f"go{t}"), 1)
                pieces(68)
                take(7, stage[:, 1])
                pieces(72)
                operand("gy0", 0, 5)
                pieces(73)
                operand("gy1", 4, 6)
                pieces(76)
                dve.wait_ge(*full("dq0", layer))
                take(8, stage[:, 0])
                pieces(84)
                dve.wait_ge(*full("dq1", layer))
                take(9, stage[:, 1])

                def softmax_max(h):
                    s = source(f"score{h}")
                    if h >= 2:
                        dve.wait_ge(*full(f"w{h - 2}", layer))
                    sc = att[:, (h % 2) * 768:(h % 2 + 1) * 768].rearrange("p (m n) -> p m n", m=2)
                    mask = maskb[:].rearrange("p (o n) -> p o n", o=1).broadcast_to([P, 2, 384])
                    ins = dve.tensor_tensor(sc, s[:].rearrange("p (m n) -> p m n", m=2)[:, :, 0:384],
                                            mask, ALU.add)
                    ins.then_inc(done_sem(f"score{h}"), 1)
                    dve.wait_ge(*done(f"score{h}", layer))
                    dve.reduce_max(smax[:, h, :, 0], sc[:, :, 0:P], axis=AXX)
                    link(dve.reduce_max(smax[:, h, :, 1], sc[:, :, P:384], axis=AXX))
                    dve.tensor_scalar(nmax[:, h], smax[:, h], -SCALE, None,
                                      ALU.mult).then_inc(smax_ready, 1)

                def softmax_diff(h):
                    dve.wait_ge(exp_ready, layer * DH + (h + 1))
                    base = (h % 2) * 768
                    link(dve.reciprocal(srec[:, h], ssum[:, h]))
                    link(dve.tensor_scalar(lrec[:, h], srec[:, h, 1, :], nlam[:], None, ALU.mult))
                    parts = [(0, base, base + P), (1, base + P, base + 384)]
                    for t, a, b in parts:
                        last = dve.tensor_scalar(att[:, a + 384:b + 384], att[:, a + 384:b + 384],
                                                 lrec[:, h, t:t + 1], None, ALU.mult)
                    link(last)
                    for t, a, b in parts:
                        last = dve.scalar_tensor_tensor(out=att[:, a:b], in0=att[:, a:b],
                                                        scalar=srec[:, h, 0, t:t + 1],
                                                        in1=att[:, a + 384:b + 384],
                                                        op0=ALU.mult, op1=ALU.add)
                    last.then_inc(w_ready, 1)

                def head_norm(h):
                    s = source(f"do{h}")
                    dve.wait_ge(o_rs, layer * DH + (h + 1))
                    for t in range(T):
                        last = dve.scalar_tensor_tensor(out=y[:, t, h * 256:(h + 1) * 256],
                                                        in0=s[:, t * 256:(t + 1) * 256],
                                                        scalar=ors[:, h, t:t + 1], in1=subw[:],
                                                        op0=ALU.mult, op1=ALU.mult)
                    last.then_inc(done_sem(f"do{h}"), 1)

                def mixed(k):
                    chunk_ready(12 + k)
                    add_to_x(k % 2, k % 4)

                pieces(88)
                softmax_max(0)
                pieces(90)
                softmax_diff(0)
                pieces(92)
                softmax_max(1)
                take(10, v[:, :, 0:CW])
                pieces(94)
                softmax_diff(1)
                pieces(95)
                softmax_max(2)
                pieces(98)
                head_norm(0)
                softmax_diff(2)
                pieces(100)
                softmax_max(3)
                take(11, v[:, :, CW:1024])
                pieces(103)
                head_norm(1)
                softmax_diff(3)
                pieces(104)
                mixed(0)
                pieces(107)
                head_norm(2)
                pieces(108)
                mixed(1)
                pieces(110)
                head_norm(3)
                operand("dy0", 8, 7)
                pieces(112)
                mixed(2)
                pieces(113)
                operand("dy1", 12, 8)
                for k in range(3, 7):
                    pieces(104 + 4 * k)
                    mixed(k)
                    if k in (4, 5):
                        pieces(106 + 4 * k)
                        normed_low(f"m{k - 4}", k - 4, 16, 9 + k - 4)

                def mlp_block(blk, is_first):
                    before = layer * LAYER_PIECES + blk * BLOCK_PIECES + MIX_PIECES
                    highs = layer * (len(OPERANDS) + HUSES) + blk * 4 + len(OPERANDS)
                    for r in range(BLOCK_PIECES):
                        if is_first and r == 2:
                            normed_low("m2", 2, 16, 11)
                        if is_first and r == 6:
                            normed_low("m3", 3, 16, 12)
                        if r == 3:
                            dve.wait_ge(piece_used, before + SLOTS)
                            add_to_x(1, 3)
                        if r % 8 == 3 and r > 8:
                            c = r // 8 - 1
                            dve.wait_ge(piece_used, before + (SLOTS + IN_CHUNK * (c + 1)))
                            if c < 4:
                                if is_first and c == 0:
                                    dve.wait_ge(x_rs, layer * 2 + 2)
                                for t in range(T):
                                    last = dve.tensor_scalar(stage[:, c % 2, t, :], acc[c % 2][:, t, :],
                                                             xrs[:, 1, t:t + 1], 0.0, ALU.mult, ALU.max)
                                last.then_inc(acc_done, 1)
                            else:
                                add_to_x(c % 2, c - 4)
                        if r % 8 == 6 and 8 < r <= 38:
                            c = r // 8 - 1
                            dve.wait_ge(side_full[hpair(c)], hnth(c, blk, layer))
                            dve.wait_ge(side_high, highs + (c + 1))
                            dve.tensor_tensor(
                                mt_low[:, 4 * c:4 * c + 4, :].rearrange("p a b -> p (a b)"),
                                side[hpair(c)][:],
                                mt_high[:, 4 * c:4 * c + 4, :].rearrange("p a b -> p (a b)").bitcast(F32),
                                ALU.subtract).then_inc(side_done[hpair(c)], 1)
                        split(r, before)

                mlp_block(0, True)
                with dve.Fori(1, BLOCKS) as blk:
                    mlp_block(blk, False)
                dve.wait_ge(piece_used, layer * LAYER_PIECES + (LAYER_PIECES + SLOTS))
                add_to_x(1, 3)
                link.end_layer()

        @block.gpsimd
        def _(pool):
            link = Chain(pool, pool_step, STEPS["pool"])
            pool.memset(mt_high[:, :, 0:P].bitcast(F32), 0.0)
            pool.memset(mt_low[:, :, 0:P].bitcast(F32), 0.0)
            pool.memset(neghalf[:], -0.5)
            pool.memset(eps[:], EPS)
            pool.memset(sub_eps[:], SUB_EPS).then_inc(const_ready, 1)
            pool.wait_ge(const_ready, 1)

            def rsqrt(dst, mid, src, signal, sub=False):
                n = src.shape[-1]
                link(pool.tensor_tensor(mid, src, (sub_eps if sub else eps)[:, 0:n], ALU.add))
                return pool.tensor_tensor(dst, mid, neghalf[:, 0:n], ALU.pow).then_inc(signal, 1)

            with pool.Fori(0, DEPTH) as layer:
                link.start_layer(layer, 0)
                pool.wait_ge(params_in, layer * (PARAM_DMAS * 16) + PARAM_DMAS * 16)
                pool.wait_ge(x_ss, layer * (2 * T) + T)
                rsqrt(xrs[:, 0, :], xrs0[:], xss[:], x_rs)
                pool.memset(att[:, 0:1024], 0.0).then_inc(att_zero, 1)

                def level(n):
                    pool.wait_ge(lev_exp, layer * 8 + (n + 1))
                    if n == 0:
                        pool.wait_ge(*done("gq", layer))
                        pool.wait_ge(*done("gk", layer))
                    if n >= 2:
                        pool.wait_ge(*full(f"level{n - 2}", layer))
                    e, ql, kl = expo[:, n % 2], q_lev[:, n % 2, :], k_lev[:, n % 2]
                    if n == 0:
                        pool.tensor_tensor(ql.rearrange("p (h i) -> p h i", h=GH), gq_t[:, :, P:SEQ],
                                           e[:, :, P:SEQ], ALU.mult)
                        pool.tensor_tensor(kl[:, :, 0:P], gk_t[:, :, 0:P], e[:, :, 0:P],
                                           ALU.mult).then_inc(lev_ready, 1)
                        return
                    half = P >> n
                    e_left, e_right, _ = halves(flat(e), half)
                    pool.tensor_tensor(ql.rearrange("p (n s) -> p n s", s=half),
                                       halves(flat(gq_t[:]), half)[1], e_right, ALU.mult)
                    if n == 1 or n == 2:
                        pool.tensor_tensor(flat(kl), flat(gk_t[:]), flat(e), ALU.mult).then_inc(lev_ready, 1)
                    else:
                        pool.tensor_tensor(halves(flat(kl), half)[0], halves(flat(gk_t[:]), half)[0],
                                           e_left, ALU.mult).then_inc(lev_ready, 1)

                def gate(c):
                    pool.wait_ge(gate_rec, layer * (2 * T) + T * (c + 1))
                    g = y[:, :, c * CW:(c + 1) * CW]
                    link(pool.tensor_tensor(g, g, stage[:, c], ALU.mult))
                    g4 = g.rearrange("p t (h d) -> p t h d", h=2)
                    w = onw[:].rearrange("p (a b d) -> p a b d", a=1, b=1).broadcast_to([P, T, 2, DV])
                    pool.tensor_tensor(g4, g4, w, ALU.mult).then_inc(gate_ready, 1)

                for n in range(3):
                    level(n)
                pool.wait_ge(trig_ready, layer * 2 + 2)
                for n in range(2):
                    wa = qknw[:, n, 0:64].rearrange("p (o f) -> p o f", o=1).broadcast_to([P, T, 64])
                    wb = qknw[:, n, 64:P].rearrange("p (o f) -> p o f", o=1).broadcast_to([P, T, 64])
                    pool.tensor_tensor(rope_c[:, n, :, 0:64], cosb[:], wa, ALU.mult)
                    pool.tensor_tensor(rope_c[:, n, :, 64:P], cosb[:], wb, ALU.mult)
                    pool.tensor_tensor(rope_s[:, n, :, 0:64], nsin[:], wb, ALU.mult)
                    last = pool.tensor_tensor(rope_s[:, n, :, 64:P], sinb[:], wa, ALU.mult)
                link(last)
                for n in range(3, 6):
                    level(n)
                level(6)
                gate(0)
                level(7)
                gate(1)
                for t in range(T):
                    pool.wait_ge(g_ss, layer * T + (t + 1))
                    rsqrt(grs[:, t, :], grs0[:, t, :], gss[:, t, :], g_rs)

                def turn(n):
                    pool.wait_ge(qk_ss, layer * 4 + (n + 1))
                    link(pool.tensor_tensor(drs0[:, n, :], dss[:, n, :], eps[:], ALU.add))
                    link(pool.tensor_tensor(drs[:, n, :], drs0[:, n, :], neghalf[:], ALU.pow))
                    st = stage[:, n % 2].rearrange("p t (j d) -> p t j d", d=P)
                    rs = drs[:, n, :].rearrange("p (t j o) -> p t j o", t=T, o=1).broadcast_to(
                        [P, T, 4, P])
                    link(pool.tensor_tensor(st, st, rs, ALU.mult))

                    def table(tab, a, b):
                        return tab[:, n // 2, :, a:b].rearrange("p t (o d) -> p t o d", o=1).broadcast_to(
                            [P, T, 4, b - a])
                    straight = tmp[:, 0:1024].rearrange("p (t j d) -> p t j d", t=T, d=P)
                    crossed = tmp[:, 1024:2048].rearrange("p (t j d) -> p t j d", t=T, d=P)
                    pool.tensor_tensor(straight, st, table(rope_c, 0, P), ALU.mult)
                    pool.tensor_tensor(crossed[:, :, :, 0:64], st[:, :, :, 64:P],
                                       table(rope_s, 0, 64), ALU.mult)
                    link(pool.tensor_tensor(crossed[:, :, :, 64:P], st[:, :, :, 0:64],
                                            table(rope_s, 64, P), ALU.mult))
                    pool.tensor_tensor(stage[:, n % 2].rearrange("p t c -> p (t c)"), tmp[:, 0:1024],
                                       tmp[:, 1024:2048], ALU.add).then_inc(rope_ready, 1)

                for n in range(4):
                    turn(n)
                for h in range(DH):
                    pool.wait_ge(o_ss, layer * DH + (h + 1))
                    rsqrt(ors[:, h, :], ors0[:, h, :], oss[:, h, :], o_rs, sub=True)
                pool.wait_ge(x_ss, layer * (2 * T) + 2 * T)
                rsqrt(xrs[:, 1, :], xrs0[:], xss[:], x_rs)
                link.end_layer()


OPERANDS = ["x0", "x1", "x2", "x3", "gy0", "gy1", "dy0", "dy1", "m0", "m1", "m2", "m3"]

NAMES = ["x", "positions", "attn_norm_w", "w_in", "gla_gate_w2", "gla_gate_b", "gla_out_norm_w",
         "diff_q_norm_w", "diff_k_norm_w", "diff_lambda_q1", "diff_lambda_k1", "diff_lambda_q2",
         "diff_lambda_k2", "diff_subln_w", "w_out", "mlp_norm_w", "w_up", "w_down"]


def constants():
    i = np.arange(P)
    causal = np.where(i[:, None] >= i[None, :], 0.0, MASKED).astype(np.float32)
    maskb = np.concatenate([causal, np.zeros((P, P), np.float32), causal], axis=1)
    lmask = np.zeros((P, 7 * 64 + P), np.float32)
    for n in range(1, 8):
        half = P >> n
        for col in range(64):
            start = col // half * 2 * half
            lmask[start:start + half, (n - 1) * 64 + col] = 1
    lmask[:, 448:] = np.eye(P, dtype=np.float32)
    scanm = np.ones((P, SEQ), np.float32)
    scanm[:, ::64] = 0.0
    invf = (np.float32(THETA) ** (-np.arange(0, 128, 2, dtype=np.float32) / np.float32(128)))
    init = [0.8 - 0.6 * math.exp(-0.3 * layer) for layer in range(DEPTH)]
    lamc = np.array([[v, 1.0 - v] for v in init], np.float32)
    return {"c_ident": np.eye(P, dtype=np.float32), "c_maskb": maskb, "c_lmask": lmask,
            "c_scanm": scanm, "c_invf": np.tile(invf.astype(np.float32), (P, 1)), "c_lamc": lamc}


def kernel(**inputs):
    import concourse.bacc as bacc
    from concourse.bass_utils import run_bass_kernel_spmd

    nc = bacc.Bacc("TRN2", target_bir_lowering=False, num_devices=1)
    arrays = {f"in_{n}": np.ascontiguousarray(inputs[n]) for n in NAMES}
    arrays.update(constants())
    args = [nc.dram_tensor(n, a.shape, mybir.dt.from_np(a.dtype), kind="ExternalInput").ap()
            for n, a in arrays.items()]
    out = nc.dram_tensor("out", (1, SEQ, D), F32, kind="ExternalOutput").ap()
    build(nc, args, out)
    r = run_bass_kernel_spmd(nc, [arrays], core_ids=[0])
    return r.results[0]["out"]
```
